# Optimizing a Trainium2 kernel written in Bass

```python
import jax, jax.numpy as jnp
from jax import lax
import numpy as np

D_MODEL = 1024
BATCH = 1
SEQ = 128
DEPTH = 2
DEC_BATCH = 1
DEC_SEQ = 128
PAST_LEN = 128

GRID_W = 64
HEAD_DIM = 64
POOL_GROUPS = 4
POOL_CH = 64
POOL_WIDTH = POOL_GROUPS * POOL_CH
POOL_WINDOWS = (2, 4, 8, 16)
H_B = 6
KV_B = 2
H_C = 6
WIN_R = 8
WIN_C = 16
Q_BLOCK = 128
ROPE_THETA = 10000.0
MIX_WIDTH = POOL_WIDTH + (H_B + H_C) * HEAD_DIM
PROJ_SIZES = (POOL_WIDTH, H_B * HEAD_DIM, KV_B * HEAD_DIM, KV_B * HEAD_DIM,
              H_C * HEAD_DIM, H_C * HEAD_DIM, H_C * HEAD_DIM)
PROJ_WIDTH = int(sum(PROJ_SIZES))
PROJ_SPLITS = [int(s) for s in np.cumsum(PROJ_SIZES)[:-1]]
N_GROUPS = 4
EXPERTS_PER_GROUP = 8
N_EXPERTS = N_GROUPS * EXPERTS_PER_GROUP
TOP_K = 2
D_EXPERT = 256
ALPHA = (2 * DEPTH) ** 0.25
BETA = (8 * DEPTH) ** -0.25
LN_EPS = 1e-6
RMS_EPS = 1e-6
NEG = -1e30

kernel_name = 'hybrid_pool_gqa_natten_hmoe_step'

def layer_norm(x, g, b):
    xf = x.astype(jnp.float32)
    mu = jnp.mean(xf, axis=-1, keepdims=True)
    var = jnp.mean(jnp.square(xf - mu), axis=-1, keepdims=True)
    return ((xf - mu) * lax.rsqrt(var + LN_EPS) * g + b).astype(x.dtype)

def rms_norm(x, w):
    xf = x.astype(jnp.float32)
    return (xf * lax.rsqrt(jnp.mean(jnp.square(xf), axis=-1, keepdims=True) + RMS_EPS) * w).astype(x.dtype)

def adaln(cvec, w, b):
    m = (jax.nn.silu(cvec) @ w + b)[..., None, :]
    return jnp.split(m, 6, axis=-1)

def rope_2d(x):
    L = x.shape[1]
    t = jnp.arange(L)
    row, col = t // GRID_W, t % GRID_W
    half = HEAD_DIM // 2
    nf = half // 2
    inv = ROPE_THETA ** (-jnp.arange(nf, dtype=jnp.float32) / nf)

    def rot(xp, pos):
        ang = pos.astype(jnp.float32)[:, None] * inv[None, :]
        cos, sin = jnp.cos(ang)[None, :, None, :], jnp.sin(ang)[None, :, None, :]
        x1, x2 = xp[..., :nf], xp[..., nf:]
        return jnp.concatenate([x1 * cos - x2 * sin, x1 * sin + x2 * cos], axis=-1)

    xf = x.astype(jnp.float32)
    return jnp.concatenate([rot(xf[..., :half], row), rot(xf[..., half:], col)], axis=-1).astype(x.dtype)

def split_proj(h, w_in):
    B, L, _ = h.shape
    a, qb, kb, vb, qc, kc, vc = jnp.split(h @ w_in, PROJ_SPLITS, axis=-1)
    r = lambda t, n: t.reshape(B, L, n, HEAD_DIM)
    return a, r(qb, H_B), r(kb, KV_B), r(vb, KV_B), r(qc, H_C), r(kc, H_C), r(vc, H_C)

def pool_mixer(a, pool_w, pool_scale):
    B, L, _ = a.shape
    ag = a.reshape(B, L, POOL_GROUPS, POOL_CH).astype(jnp.float32)
    cs = jnp.concatenate([jnp.zeros((B, 1, POOL_GROUPS, POOL_CH), jnp.float32),
                          jnp.cumsum(ag, axis=1)], axis=1)
    t = jnp.arange(L)
    outs = []
    for g, win in enumerate(POOL_WINDOWS):
        lo = jnp.clip(t - win // 2, 0, L)
        hi = jnp.clip(t + win // 2, 0, L)
        csg = cs[:, :, g]
        cnt = (hi - lo).astype(jnp.float32)[None, :, None]
        outs.append((csg[:, hi] - csg[:, lo]) / cnt - ag[:, :, g])
    pooled = jnp.stack(outs, axis=2).astype(a.dtype)
    y = jnp.einsum('blgc,gcd->blgd', pooled, pool_w)
    return y.reshape(B, L, POOL_WIDTH) * pool_scale

def blocked_attention(q, k, v):
    B, Lq, H, D = q.shape
    KVH = k.shape[2]
    G = H // KVH
    nb = Lq // Q_BLOCK
    scale = D ** -0.5
    qb = q.reshape(B, nb, Q_BLOCK, KVH, G, D).transpose(1, 0, 2, 3, 4, 5)

    def one(qblk):
        s = jnp.einsum('bqhgd,bkhd->bhgqk', qblk, k).astype(jnp.float32) * scale
        p = jax.nn.softmax(s, axis=-1).astype(v.dtype)
        return jnp.einsum('bhgqk,bkhd->bqhgd', p, v)

    o = lax.map(one, qb)
    return o.transpose(1, 0, 2, 3, 4, 5).reshape(B, Lq, H * D)

def neighborhood_attention(q, k, v, k_ctx, v_ctx, rpb):
    B, L, H, D = q.shape
    rows = L // GRID_W
    wr = min(WIN_R, rows)
    scale = D ** -0.5
    qg = q.reshape(B, rows, GRID_W, H, D)
    kg = k.reshape(B, rows, GRID_W, H, D)
    vg = v.reshape(B, rows, GRID_W, H, D)
    r = jnp.arange(rows)
    rs = jnp.clip(r - wr // 2, 0, rows - wr)
    ridx = rs[:, None] + jnp.arange(wr)[None, :]
    kr = kg[:, ridx]
    vr = vg[:, ridx]
    cidx = jnp.arange(GRID_W)
    cs = jnp.clip(cidx - WIN_C // 2, 0, GRID_W - WIN_C)
    col_ok = (cidx[None, :] >= cs[:, None]) & (cidx[None, :] < cs[:, None] + WIN_C)
    dr = ridx - r[:, None]
    dc = jnp.clip(cidx[None, :] - cidx[:, None], -(WIN_C - 1), WIN_C - 1)
    bias = rpb[:, dr[:, None, :, None] + (WIN_R - 1), dc[None, :, None, :] + (WIN_C - 1)]
    s_loc = jnp.einsum('brqhd,brjwhd->bhrqjw', qg, kr).astype(jnp.float32) * scale + bias[None].astype(jnp.float32)
    s_loc = jnp.where(col_ok[:, None, :], s_loc, NEG)
    s_ctx = jnp.einsum('brqhd,bkhd->bhrqk', qg, k_ctx).astype(jnp.float32) * scale
    P = k_ctx.shape[1]
    s = jnp.concatenate([s_loc.reshape(B, H, rows, GRID_W, wr * GRID_W), s_ctx], axis=-1)
    p = jax.nn.softmax(s, axis=-1).astype(v.dtype)
    p_loc = p[..., :wr * GRID_W].reshape(B, H, rows, GRID_W, wr, GRID_W)
    p_ctx = p[..., wr * GRID_W:]
    o = jnp.einsum('bhrqjw,brjwhd->brqhd', p_loc, vr) + jnp.einsum('bhrqk,bkhd->brqhd', p_ctx, v_ctx)
    return o.reshape(B, L, H * D)

def hier_moe(h, p):
    B, L, D = h.shape
    t = h.reshape(-1, D)
    lg = (t @ p['router_g'] + p['router_g_b']).astype(jnp.float32)
    pg = jax.nn.softmax(lg, axis=-1)
    _, gsel = lax.top_k(lg, 1)
    pg_sel = jnp.take_along_axis(pg, gsel, axis=1)
    le = (t @ p['router_e'] + p['router_e_b']).astype(jnp.float32).reshape(-1, N_GROUPS, EXPERTS_PER_GROUP)
    le_sel = jnp.take_along_axis(le, gsel[:, :, None], axis=1)[:, 0]
    ev, ei = lax.top_k(le_sel, TOP_K)
    wts = jax.nn.softmax(ev, axis=-1) * pg_sel
    eidx = gsel * EXPERTS_PER_GROUP + ei
    gate = jnp.sum(jax.nn.one_hot(eidx, N_EXPERTS, dtype=jnp.float32) * wts[..., None], axis=1).astype(h.dtype)
    hg = jnp.einsum('td,edf->tef', t, p['w_gate'])
    hu = jnp.einsum('td,edf->tef', t, p['w_up'])
    act = jax.nn.silu(hg) * hu * gate[:, :, None]
    return jnp.einsum('tef,efd->td', act, p['w_down']).reshape(B, L, D)

def residual_tail(x, ya, yb, yc, g1, sh2, sc2, g2, p):
    o = jnp.concatenate([ya, yb, yc], axis=-1) @ p['w_out']
    x = layer_norm(ALPHA * x + g1 * o, p['ln1_g'], p['ln1_b'])
    h = x * (1 + sc2) + sh2
    return layer_norm(ALPHA * x + g2 * hier_moe(h, p), p['ln2_g'], p['ln2_b'])

def context_layer(x, c_ctx, p):
    sh1, sc1, g1, sh2, sc2, g2 = adaln(c_ctx, p['w_ada'], p['b_ada'])
    h = x * (1 + sc1) + sh1
    a, qb, kb, vb, qc, kc, vc = split_proj(h, p['w_in'])
    ya = pool_mixer(a, p['pool_w'], p['pool_scale'])
    qb = rms_norm(qb, p['q_norm'])
    kb = rms_norm(kb, p['k_norm'])
    yb = blocked_attention(qb, kb, vb)
    yc = blocked_attention(qc, kc, vc)
    x = residual_tail(x, ya, yb, yc, g1, sh2, sc2, g2, p)
    return x, kb, vb, kc, vc

def latent_layer(x, c, ck_b, cv_b, ck_c, cv_c, p):
    sh1, sc1, g1, sh2, sc2, g2 = adaln(c, p['w_ada'], p['b_ada'])
    h = x * (1 + sc1) + sh1
    a, qb, kb, vb, qc, kc, vc = split_proj(h, p['w_in'])
    ya = pool_mixer(a, p['pool_w'], p['pool_scale'])
    qb = rope_2d(rms_norm(qb, p['q_norm']))
    kb = rope_2d(rms_norm(kb, p['k_norm']))
    yb = blocked_attention(qb, jnp.concatenate([ck_b, kb], axis=1), jnp.concatenate([cv_b, vb], axis=1))
    yc = neighborhood_attention(qc, kc, vc, ck_c, cv_c, p['rpb'])
    return residual_tail(x, ya, yb, yc, g1, sh2, sc2, g2, p)

def setup_inputs(seed: int = 0) -> dict:
    key = jax.random.key(seed)
    ks = jax.random.split(key, 28)
    f32 = jnp.float32
    nrm = lambda k, shape, s: jax.random.normal(k, shape, f32) * s
    D = D_MODEL
    return {
        'x_prompt': nrm(ks[0], (BATCH, SEQ, D), 1.0),
        'x_sample': nrm(ks[1], (DEC_BATCH, DEC_SEQ, D), 1.0),
        'cache_b_k': nrm(ks[2], (DEC_BATCH, DEPTH, PAST_LEN, KV_B, HEAD_DIM), 1.0),
        'cache_b_v': nrm(ks[3], (DEC_BATCH, DEPTH, PAST_LEN, KV_B, HEAD_DIM), 1.0),
        'cache_c_k': nrm(ks[4], (DEC_BATCH, DEPTH, PAST_LEN, H_C, HEAD_DIM), 1.0),
        'cache_c_v': nrm(ks[5], (DEC_BATCH, DEPTH, PAST_LEN, H_C, HEAD_DIM), 1.0),
        'c': nrm(ks[6], (DEC_BATCH, D), 1.0),
        'c_ctx': nrm(ks[7], (D,), 1.0),
        'w_ada': nrm(ks[8], (DEPTH, D, 6 * D), 0.5 * D ** -0.5),
        'b_ada': nrm(ks[9], (DEPTH, 6 * D), 0.02),
        'w_in': nrm(ks[10], (DEPTH, D, PROJ_WIDTH), D ** -0.5),
        'w_out': nrm(ks[11], (DEPTH, MIX_WIDTH, D), BETA * MIX_WIDTH ** -0.5),
        'pool_w': nrm(ks[12], (DEPTH, POOL_GROUPS, POOL_CH, POOL_CH), POOL_CH ** -0.5),
        'pool_scale': 1.0 + nrm(ks[13], (DEPTH, POOL_WIDTH), 0.02),
        'q_norm': 1.0 + nrm(ks[14], (DEPTH, HEAD_DIM), 0.02),
        'k_norm': 1.0 + nrm(ks[15], (DEPTH, HEAD_DIM), 0.02),
        'rpb': nrm(ks[16], (DEPTH, H_C, 2 * WIN_R - 1, 2 * WIN_C - 1), 0.1),
        'ln1_g': 1.0 + nrm(ks[17], (DEPTH, D), 0.02),
        'ln1_b': nrm(ks[18], (DEPTH, D), 0.02),
        'ln2_g': 1.0 + nrm(ks[19], (DEPTH, D), 0.02),
        'ln2_b': nrm(ks[20], (DEPTH, D), 0.02),
        'router_g': nrm(ks[21], (DEPTH, D, N_GROUPS), D ** -0.5),
        'router_g_b': nrm(ks[22], (DEPTH, N_GROUPS), 0.01),
        'router_e': nrm(ks[23], (DEPTH, D, N_EXPERTS), D ** -0.5),
        'router_e_b': nrm(ks[24], (DEPTH, N_EXPERTS), 0.01),
        'w_gate': nrm(ks[25], (DEPTH, N_EXPERTS, D, D_EXPERT), D ** -0.5),
        'w_up': nrm(ks[26], (DEPTH, N_EXPERTS, D, D_EXPERT), D ** -0.5),
        'w_down': nrm(ks[27], (DEPTH, N_EXPERTS, D_EXPERT, D), BETA * D_EXPERT ** -0.5),
    }

def reference(x_prompt, x_sample, cache_b_k, cache_b_v, cache_c_k, cache_c_v, c, c_ctx,
              w_ada, b_ada, w_in, w_out, pool_w, pool_scale, q_norm, k_norm, rpb,
              ln1_g, ln1_b, ln2_g, ln2_b, router_g, router_g_b, router_e, router_e_b,
              w_gate, w_up, w_down):
    xp = x_prompt
    xs = x_sample
    kb_list, vb_list, kc_list, vc_list = [], [], [], []
    for l in range(DEPTH):
        p = {'w_ada': w_ada[l], 'b_ada': b_ada[l], 'w_in': w_in[l], 'w_out': w_out[l],
             'pool_w': pool_w[l], 'pool_scale': pool_scale[l], 'q_norm': q_norm[l], 'k_norm': k_norm[l],
             'rpb': rpb[l], 'ln1_g': ln1_g[l], 'ln1_b': ln1_b[l], 'ln2_g': ln2_g[l], 'ln2_b': ln2_b[l],
             'router_g': router_g[l], 'router_g_b': router_g_b[l], 'router_e': router_e[l],
             'router_e_b': router_e_b[l], 'w_gate': w_gate[l], 'w_up': w_up[l], 'w_down': w_down[l]}
        xp, kb, vb, kc, vc = context_layer(xp, c_ctx, p)
        kb_list.append(kb)
        vb_list.append(vb)
        kc_list.append(kc)
        vc_list.append(vc)
        xs = latent_layer(xs, c, cache_b_k[:, l], cache_b_v[:, l], cache_c_k[:, l], cache_c_v[:, l], p)
    new_b_k = jnp.stack(kb_list, axis=1)
    new_b_v = jnp.stack(vb_list, axis=1)
    new_c_k = jnp.stack(kc_list, axis=1)
    new_c_v = jnp.stack(vc_list, axis=1)
    return (xp, xs, new_b_k, new_b_v, new_c_k, new_c_v)


_drawn_inputs = setup_inputs


def setup_inputs(seed=0):
    import zlib

    import numpy as np

    out = dict(_drawn_inputs(seed))
    spreads = {}
    factors = {'cache_b_k': 8.0,
     'cache_b_v': 8.0,
     'cache_c_k': 6.048,
     'cache_c_v': 4.846,
     'pool_scale': 22.938,
     'q_norm': 8.0,
     'k_norm': 7.761,
     'rpb': 64.0,
     'router_g_b': 22.938,
     'router_e_b': 29.883}
    for name, (base, spread) in spreads.items():
        noise = np.random.default_rng([zlib.crc32(name.encode()), seed]).standard_normal(out[name].shape)
        drawn = base * np.exp(spread * noise) if base else spread * noise
        out[name] = __import__('jax').numpy.asarray(drawn.astype(out[name].dtype))
    for name, factor in factors.items():
        out[name] = (out[name] * factor).astype(out[name].dtype)
    return out
```

```python
from contextlib import ExitStack

import concourse.bass as bass
import numpy as np
from concourse import mybir

ALU = mybir.AluOpType
ACT = mybir.ActivationFunctionType
AX = mybir.AxisListType
F32 = mybir.dt.float32
I32 = mybir.dt.int32
BF16 = mybir.dt.bfloat16

P = 128
D = 1024
KT = D // P
DEPTH = 2
HD = 64
NPAIR = 3
VECS = 6
UNIT = 2048
UC = UNIT // KT
SLOTS = 12
NE = 32
NG = 4
FE = 256
BLK = 32
PAIRS = 2 * 2 * P
SORTED = PAIRS + BLK
HALF = PAIRS // 2
CHUNKS = ((0, 512), (512, D))
ROUND = SLOTS // 3
LAST_ROUND = NE // ROUND - 1
ALPHA = (2 * DEPTH) ** 0.25
EPS = 1e-6
ROW_ORDER = (1, 0, 2, 4, 3, 5)
MIXER_UNITS = 8 + 8 + 16 + 4
CA, CQB, CKB, CVB, CQC, CKC, CVC = 0, 256, 640, 768, 896, 1280, 1664
POOL_WINDOWS = (2, 4, 8, 16)
GRID_W, WIN_C = 64, 16
RPB_ROWS, RPB_COLS = 15, 31
BIG = 1e30

CONSTS = {}
_at = 0
for _name, _n in (("ident", P), ("part", 2), ("rows", 8), ("iota", PAIRS), ("before", P), ("ones", NE), ("pool", 4 * P),
                  ("cos", HD), ("sin", HD), ("flip", P), ("mask", P), ("fold", 2 * BLK), ("rank_g", NG),
                  ("rank_e", NE), ("steps", 8), ("power", 8)):
    CONSTS[_name] = (_at, _n)
    _at += _n
CONST_COLS = _at
FIRST_CONSTS = CONSTS["iota"][0]


def shape_constants():
    t = np.zeros((P, CONST_COLS), np.float32)

    def put(name, value):
        a, n = CONSTS[name]
        t[:, a:a + n] = value

    i = np.arange(P)
    put("ident", np.eye(P))
    put("iota", np.arange(PAIRS)[None, :])
    put("before", i[:, None] < i[None, :])
    put("ones", 1.0)
    pool = np.zeros((P, 4, P), np.float32)
    for g, win in enumerate(POOL_WINDOWS):
        lo, hi = np.clip(i - win // 2, 0, P), np.clip(i + win // 2, 0, P)
        inside = (i[:, None] >= lo[None, :]) & (i[:, None] < hi[None, :])
        pool[:, g, :] = inside / (hi - lo).astype(np.float32)[None, :] - np.eye(P)
    put("pool", pool.reshape(P, 4 * P))
    nf = HD // 4
    inv = (10000.0 ** (-np.arange(nf, dtype=np.float32) / nf)).astype(np.float32)
    row = (i // GRID_W).astype(np.float32)[:, None] * inv[None, :]
    col = (i % GRID_W).astype(np.float32)[:, None] * inv[None, :]
    put("cos", np.concatenate([np.cos(row), np.cos(row), np.cos(col), np.cos(col)], 1))
    put("sin", np.concatenate([-np.sin(row), np.sin(row), -np.sin(col), np.sin(col)], 1))
    put("flip", i[None, :] == (i - i % GRID_W + GRID_W - 1 - i % GRID_W)[:, None])
    c = i % GRID_W
    first = np.clip(c - WIN_C // 2, 0, GRID_W - WIN_C)
    ok = (c[None, :] >= first[:, None]) & (c[None, :] < first[:, None] + WIN_C)
    put("mask", np.where(ok, 0.0, -BIG))
    fold = np.zeros((P, 2, BLK), np.float32)
    for p in range(P):
        fold[p, p // BLK // 2, p % BLK] = 1.0
    put("fold", fold.reshape(P, 2 * BLK))
    put("rank_g", (NG - np.arange(NG))[None, :])
    put("rank_e", (NE - np.arange(NE))[None, :])
    put("steps", np.concatenate([[-1], BLK * np.arange(1, 8)])[None, :])
    put("power", -0.5)
    part = i % 32 // 2
    put("part", np.stack([-(part >= 1).astype(np.float32), -(part >= 2).astype(np.float32)], 1))
    rows = np.zeros((P, 2, 4), np.float32)
    for p in range(P):
        if p % 32 < 6:
            rows[p, p % 2, p // 32] = 1.0
    put("rows", rows.reshape(P, 8))
    return t


def backbone(nc, x_prompt, x_sample, cache_b_k, cache_b_v, cache_c_k, cache_c_v, c, c_ctx, w_ada, b_ada, w_in,
             w_out, pool_w, pool_scale, q_norm, k_norm, rpb, ln1_g, ln1_b, ln2_g, ln2_b, router_g, router_g_b,
             router_e, router_e_b, w_gate, w_up, w_down, consts, y_prompt, y_sample, new_b_k, new_b_v, new_c_k,
             new_c_v):
    with ExitStack() as ctx:
        def sb(name, shape, dt=F32):
            return ctx.enter_context(nc.sbuf_tensor(name, shape, dt))

        def sem(name):
            return ctx.enter_context(nc.semaphore(name))

        ring = sb("ring", [P, SLOTS * UNIT])
        X = sb("X", [P, 2, D])
        area_a = sb("area_a", [P, KT * SORTED])
        area_b = sb("area_b", [P, KT * SORTED])
        area_c = sb("area_c", [P, 3072])
        mixT = sb("mixT", [P, KT, 2 * P])
        K = sb("K", [P, CONST_COLS])
        bias_rows = sb("bias_rows", [P, VECS, UC])
        R = sb("R", [P, VECS, UC], BF16)
        part16 = sb("part16", [P, UC], BF16)
        rows16 = sb("rows16", [P, 8], BF16)
        KM = [sb("KM0", [P, 4, 2, P]), sb("KM1", [P, 4, 2, 2 * P])]
        cvec = sb("cvec", [P, 2, KT])
        CS = sb("CS", [P, KT, BLK])
        relb = sb("relb", [P, 6, P])
        ck_b = sb("ck_b", [P, P]); cv_b = sb("cv_b", [P, P])
        ck_c = sb("ck_c", [P, 3 * P]); cv_c = sb("cv_c", [P, 3 * P])
        qk_w = sb("qk_w", [P, 2, HD])
        poolw = sb("poolw", [P, 2, P])
        pools = sb("pools", [P, 2])
        ln1_rows = sb("ln1_rows", [P, 2, UC])
        rw = sb("rw", [P, KT, NG + NE])
        rb = sb("rb", [P, NG + NE])
        nmx = sb("nmx", [P, 24]); sums = sb("sums", [P, 24]); rsum = sb("rsum", [P, 24])
        st = sb("st", [P, 64])
        LG = sb("LG", [P, 2, NG + NE])
        ga = sb("ga", [P, 2, NG]); gb = sb("gb", [P, 2, NG])
        ea = sb("ea", [P, 2, NE]); LE = sb("LE", [P, 2, NE])
        OH2 = sb("OH2", [P, 2, 2, NE])
        OH = [OH2[:, 0], OH2[:, 1]]
        M = sb("M", [P, 2, NE], BF16)
        before16 = sb("before16", [P, P], BF16); ones16 = sb("ones16", [P, 1], BF16)
        OP = sb("OP", [P, 2, NE])
        cnt = sb("cnt", [P, NE]); incl = sb("incl", [P, NE]); off = sb("off", [P, NE])
        sc = sb("sc", [P, 32])
        cmp8 = sb("cmp8", [1, NE, 8])
        tabf = sb("tabf", [1, 4, NE + 1])
        tab = sb("tab", [1, 3, NE + 1], I32)
        hb = sb("hb", [P, KT, BLK])
        SG = sb("SG", [P, HD]); A2 = sb("A2", [P, P]); AT = sb("AT", [P, 2 * BLK]); Yb = sb("Yb", [P, UC])

        def const(name):
            a, n = CONSTS[name]
            return K[:, a:a + n]

        ident = const("ident")
        PR = area_a[:, 0:4096].rearrange("p (s n) -> p s n", s=2)
        LN1 = area_a[:, 2048:4096].rearrange("p (v n) -> p v n", v=2)
        hS = area_a[:, :].rearrange("p (k n) -> p k n", k=KT)
        yS = area_a[:, 0:4096].rearrange("p (i n) -> p i n", i=4)
        Hn = area_b[:, KT * (HALF + BLK):].rearrange("p (s n) -> p s n", s=2)
        hT = area_b[:, 0:2048].rearrange("p (k n) -> p k n", k=KT)
        QT = area_b[:, 0:1536].rearrange("p (s i n) -> p s i n", s=2, i=6)
        ON = area_b[:, 1536:3072].rearrange("p (s h n) -> p s h n", s=2, h=12)
        QN = area_c[:, 512:1280].rearrange("p (s i r n) -> p s i r n", s=2, i=3, r=2)
        yST = area_b[:, :].rearrange("p (n k) -> p k n", k=KT)
        PX = area_c[:, 0:1024].rearrange("p (b n) -> p b n", b=2)
        PT = area_c[:, 1024:2048].rearrange("p (b n) -> p b n", b=2)
        SX = area_c[:, 2048:3072].rearrange("p (b n) -> p b n", b=2)
        T1 = area_c[:, 0:512]
        pooled = area_c[:, 2048:2560].rearrange("p (s a n) -> p s a n", s=2, a=2)
        GB = area_c[:, 0:2048].rearrange("p (s n) -> p s n", s=2)
        pick = area_c[:, 0:1024].rearrange("p (s n) -> p s n", s=2)
        pickw = area_c[:, 1024:2048].rearrange("p (s n) -> p s n", s=2)
        CT = area_c[:, 2048:3072].rearrange("p (i n) -> p i n", i=4)
        tmpw = area_c[:, 2048:2560]
        place = area_c[:, 2560:2688].rearrange("p (a s n) -> p a s n", a=2, s=2)
        LN2 = mixT[:, :, :].rearrange("p k n -> p (k n)").rearrange("p (v n) -> p v n", v=2)

        Q = [ctx.enter_context(nc.psum_tensor(f"Q{i}", [P, 1024], F32)) for i in range(4)]
        GU, ATp = Q[0][:, 0:P], Q[0][:, 512:512 + 2 * BLK]
        row_f, row_rest = Yb[:, :], hb[:, :, :].rearrange("p k n -> p (k n)")
        Yp, YTp = Q[1][:, 0:UC], Q[1][:, 512:512 + UC]

        def slot(m):
            return ring[:, (m % SLOTS) * UNIT:(m % SLOTS + 1) * UNIT]

        slot_loaded = [sem(f"slot_loaded{i}") for i in range(SLOTS)]
        c_loaded = sem("c_loaded"); consts_loaded = sem("consts_loaded"); tables_loaded = sem("tables_loaded")
        x0_loaded = sem("x0_loaded"); x1_loaded = sem("x1_loaded"); small_loaded = sem("small_loaded")
        router_loaded = sem("router_loaded"); bias_loaded = sem("bias_loaded")
        ln_loaded = sem("ln_loaded"); kv_stored = sem("kv_stored"); y_stored = sem("y_stored")
        cleared = sem("cleared"); rows_cleared = sem("rows_cleared"); cs_cleared = sem("cs_cleared")
        cs_ready = sem("cs_ready"); unit_used = sem("unit_used")
        row_ready = sem("row_ready"); bc_done = sem("bc_done")
        h_ready = sem("h_ready"); h_turned = sem("h_turned"); hT_ready0 = sem("hT_ready0")
        hT_ready1 = sem("hT_ready1")
        proj_done = sem("proj_done"); proj_kept = sem("proj_kept")
        qk_ready = sem("qk_ready"); pool_done = sem("pool_done"); pooled_kept = sem("pooled_kept")
        poolmix_done = sem("poolmix_done"); poolmix_kept = sem("poolmix_kept")
        q_turned = sem("q_turned"); k_turned = sem("k_turned"); q_kept = sem("q_kept"); k_kept = sem("k_kept")
        score_done = sem("score_done"); max_ready = sem("max_ready"); exp_done = sem("exp_done")
        p_turned = sem("p_turned"); p_kept = sem("p_kept"); pv_done = sem("pv_done"); o_kept = sem("o_kept")
        o_turned = sem("o_turned"); mix_ready0 = sem("mix_ready0"); mix_ready1 = sem("mix_ready1")
        gate_ready = sem("gate_ready")
        out_done = sem("out_done"); out_used = sem("out_used"); x_ready = sem("x_ready")
        rows_picked = sem("rows_picked")
        logits_done = sem("logits_done"); group_shift = sem("group_shift"); group_exp = sem("group_exp")
        pair_diff = sem("pair_diff"); pair_exp = sem("pair_exp")
        chosen = sem("chosen"); counted = sem("counted"); tab_ready = sem("tab_ready")
        pick_ready = sem("pick_ready")
        pickw_ready = sem("pickw_ready")
        gathered = sem("gathered"); sorted_kept = sem("sorted_kept"); w_turned = sem("w_turned")
        w_kept = sem("w_kept")
        hb_ready = sem("hb_ready"); gu_done = sem("gu_done"); sg_ready = sem("sg_ready"); a2_ready = sem("a2_ready")
        s_done = sem("s_done"); at_kept = sem("at_kept"); d_done = sem("d_done"); y_kept = sem("y_kept")
        yt_done = sem("yt_done"); yt_kept = sem("yt_kept")
        ys_turned = sem("ys_turned"); ys_kept = sem("ys_kept"); comb_done = sem("comb_done")
        var_ready = sem("var_ready"); rstd_ready = sem("rstd_ready")
        act_step = sem("act_step"); dve_step = sem("dve_step")

        def entry(e, row, i, lo, hi):
            return e.value_load(tab[0:1, row, bass.ds(i, 1)], min_val=lo, max_val=hi)

        MAXB = 2 * (NE + PAIRS // BLK) + 8

        def blocks_of_expert(e, i, body, with_start=True):
            n = entry(e, 1, i, 1, PAIRS // 2 // BLK)
            b0 = entry(e, 2, i, 0, MAXB)
            start = entry(e, 0, i, 0, PAIRS) if with_start else None
            body(b0, start, True)
            with e.If(n > 1):
                with e.Fori(1, n) as b:
                    at = nc.s_assert_within(
                        start + b * BLK, 0, PAIRS,
                        skip_runtime_bounds_check_because="a block starts inside its expert's run") if with_start else None
                    body(b0 + b, at, False)

        def key_rows(s, r):
            rows = slice(64 * r, 64 * r + 64)
            if s == 0:
                return KM[0][rows, :, r, :], Q[2][rows, 0:4 * P].rearrange("p (i n) -> p i n", i=4)
            return (KM[1][rows, :, r, :].rearrange("p i (t n) -> p t i n", t=2),
                    Q[2][rows, :].rearrange("p (t i n) -> p t i n", t=2, i=4))

        def second_half(n):
            return (hS[:, 2 * n:2 * n + 2, HALF:PAIRS],
                    Q[2 + n // 2][:, 512 * (n % 2):512 * (n % 2) + 512].rearrange("p (k n) -> p k n", k=2))

        def small(e, l):
            def load(dst, src, slow=False):
                e.dma_start(dst, src, allow_slow_non_contiguous=slow).then_inc(small_loaded, 16)
            load(ck_b[:, :], cache_b_k[0, l].rearrange("t h n -> t (h n)"))
            load(cv_b[:, :], cache_b_v[0, l].rearrange("t h n -> t (h n)"))
            load(ck_c[:, :], cache_c_k[0, l].rearrange("t h n -> t (h n)"))
            load(cv_c[:, :], cache_c_v[0, l].rearrange("t h n -> t (h n)"))
            load(qk_w[:, 0, :], q_norm[l:l + 1, :].broadcast_to([P, HD]))
            load(qk_w[:, 1, :], k_norm[l:l + 1, :].broadcast_to([P, HD]))
            for r in range(2):
                load(poolw[64 * r:64 * r + 64, :, 64 * r:64 * r + 64],
                     pool_w[l].rearrange("(a r) c d -> r c a d", r=2)[r])
            load(pools[:, :], pool_scale[l].rearrange("(a p) -> p a", p=P), slow=True)
            for row in range(6):
                for n, w in enumerate((ln1_g, ln1_b)):
                    load(ln1_rows[row:P:32, n, :], w[l].rearrange("(j n) -> j n", j=4))
            for r in range(2):
                for j in range(2):
                    at = (l * 6 * RPB_ROWS + RPB_ROWS // 2 + j - r) * RPB_COLS + RPB_COLS // 2 - (GRID_W - 1)
                    src = bass.AP(rpb.tensor, at, [[1, GRID_W], [RPB_ROWS * RPB_COLS, 6], [1, GRID_W]])
                    load(relb[64 * r:64 * r + 64, :, GRID_W * j:GRID_W * (j + 1)], src)

        def router_tables(e, l):
            for dst, src in ((rw[:, :, 0:NG], router_g[l].rearrange("(p k) e -> p k e", k=KT)),
                             (rw[:, :, NG:], router_e[l].rearrange("(p k) e -> p k e", k=KT)),
                             (rb[:, 0:NG], router_g_b[l:l + 1, :].broadcast_to([P, NG])),
                             (rb[:, NG:], router_e_b[l:l + 1, :].broadcast_to([P, NE]))):
                e.dma_start(dst, src).then_inc(router_loaded, 16)

        def biases(e, l):
            for row in range(6):
                e.dma_start(bias_rows[row:P:32, :, :], b_ada[l].rearrange("(v j n) -> j v n", v=VECS, j=4))\
                 .then_inc(bias_loaded, 16)

        block = ctx.enter_context(nc.Block())

        @block.sync
        def _(sp):
            sp.dma_start(cvec[:, 0, :], c_ctx.rearrange("(p k) -> p k", k=KT)).then_inc(c_loaded, 16)
            sp.dma_start(cvec[:, 1, :], c.rearrange("b (p k) -> (b p) k", k=KT)).then_inc(c_loaded, 16)

            def ada_unit(l, v, j):
                return w_ada[l].rearrange("(p k) n -> p k n", k=KT)[:, :, v * D + j * UC:v * D + (j + 1) * UC]

            def in_unit(l, n):
                return w_in[l].rearrange("(p k) n -> p k n", k=KT)[:, :, n * UC:(n + 1) * UC]

            def out_unit(l, n):
                return w_out[l].rearrange("(k p) n -> p k n", p=P)[:, :, n * UC:(n + 1) * UC]

            def load_expert(l, e, i):
                return [(3 * i, w_gate[l, bass.ds(e, 1)].rearrange("o (p k) f -> p (o k f)", k=KT)),
                        (3 * i + 1, w_up[l, bass.ds(e, 1)].rearrange("o (p k) f -> p (o k f)", k=KT)),
                        (3 * i + 2, w_down[l, bass.ds(e, 1)].rearrange("o (q p) d -> p (o q) d", p=P))]

            def fill(m, src):
                dst = slot(m)
                if len(src.shape) == 3:
                    dst = dst.rearrange("p (k n) -> p k n", k=src.shape[1])
                sp.dma_start(dst, src).then_inc(slot_loaded[m % SLOTS], 16)

            for l in range(DEPTH):
                units = [ada_unit(l, v, j) for v in (1, 0) for j in range(4)]
                units += [in_unit(l, n) for n in range(8)]
                units += [ada_unit(l, v, j) for v in (2, 4, 3) for j in range(4)]
                units += [out_unit(l, n) for n in range(4)]
                units += [ada_unit(l, 5, j) for j in range(4)]
                for m, src in enumerate(units):
                    if m >= SLOTS:
                        sp.wait_ge(unit_used, MIXER_UNITS * l + m - SLOTS + 1)
                    elif l:
                        after = entry(sp, 2, NE - ROUND + m // 3 + 1, 1, MAXB)
                        if m % 3 < 2:
                            sp.wait_ge(gu_done, after + 1)
                        else:
                            sp.wait_ge(d_done, after + l - 1 + 2)
                    fill(m, src)
                    if l == 0 and m == 3:
                        sp.wait_ge(rows_cleared, 1)
                        biases(sp, 0)
                        sp.dma_start(K[:, 0:FIRST_CONSTS], consts[:, 0:FIRST_CONSTS]).then_inc(consts_loaded, 16)
                    if l == 0 and m == 7:
                        sp.dma_start(X[:, 0, :], x_prompt.rearrange("b t d -> (b t) d")).then_inc(x0_loaded, 16)
                    if l == 0 and m == 9:
                        sp.dma_start(X[:, 1, :], x_sample.rearrange("b t d -> (b t) d")).then_inc(x1_loaded, 16)
                    if l == 0 and m == 15:
                        sp.dma_start(K[:, FIRST_CONSTS:], consts[:, FIRST_CONSTS:]).then_inc(tables_loaded, 16)
                        sp.wait_ge(cleared, 1)
                        small(sp, 0)
                        router_tables(sp, 0)
                for e in range(ROUND):
                    for m, src in load_expert(l, e, e):
                        if l + 1 < DEPTH and m == 4:
                            sp.wait_ge(row_ready, 6 * l + 5)
                            sp.wait_ge(pv_done, 12 * (l + 1))
                            small(sp, l + 1)
                        sp.wait_ge(unit_used, MIXER_UNITS * l + MIXER_UNITS - SLOTS + m + 1)
                        fill(m, src)
                sp.wait_ge(tab_ready, l + 1)
                if l + 1 < DEPTH:
                    sp.wait_ge(row_ready, 6 * (l + 1))
                    biases(sp, l + 1)
                    router_tables(sp, l + 1)
                with sp.Fori(1, NE // ROUND) as turn_no:
                    for i in range(ROUND):
                        after = entry(sp, 2, turn_no * ROUND + (i - ROUND + 1), 1, MAXB)
                        for m, src in load_expert(l, turn_no * ROUND + i, i):
                            if m % 3 == 0:
                                sp.wait_ge(gu_done, after + 1)
                            if m % 3 == 2:
                                sp.wait_ge(d_done, after + l + 2)
                            fill(m, src)

            for ready, s, lo, hi in ((1, 0, 0, D), (2, 1, 0, D // 2), (3, 1, D // 2, D)):
                sp.wait_ge(x_ready, 4 * DEPTH - 2 + ready)
                y = (y_prompt, y_sample)[s].rearrange("b t d -> (b t) d")
                sp.dma_start(y[:, lo:hi], X[:, s, lo:hi]).then_inc(y_stored, 16)
            sp.wait_ge(y_stored, 48)

        @block.tensor
        def _(pe):
            used = [0] * SLOTS

            def unit(m):
                used[m % SLOTS] += 1
                pe.wait_ge(slot_loaded[m % SLOTS], 16 * used[m % SLOTS])
                return slot(m).rearrange("p (k n) -> p k n", k=KT)

            def ada(l, v, m):
                js_sets = ((0, 1), (2, 3)) if l == 0 and m < 8 else (range(4),)
                bank = ROW_ORDER.index(v) % 2
                out = Q[3][:, 512 * bank:512 * bank + UC]
                for js in js_sets:
                    us = [unit(m + j) for j in js]
                    for k in range(KT):
                        for j, u in zip(js, us):
                            mm = pe.matmul(out[32 * j:32 * j + 32, :], CS[:, k, :], u[:, k, :], start=k == 0,
                                           stop=k == KT - 1)
                            if k == KT - 1:
                                mm.then_inc(unit_used, 1)

            def rows_to_all(l, v, s, dst):
                pe.wait_ge(row_ready, 6 * l + ROW_ORDER.index(v) + 1)
                for j in range(4):
                    picks = rows16[:, 4 * s + j:4 * s + j + 1].broadcast_to([P, P])
                    mm = pe.matmul(dst[:, UC * j:UC * (j + 1)], picks, R[:, v, :], start=True, stop=True)
                mm.then_inc(bc_done, 1)

            def turn(dst, srcs, signal):
                for i, src in enumerate(srcs):
                    t = pe.transpose(dst[:, P * i:P * (i + 1)], src, ident)
                t.then_inc(signal, 1)

            def turn_h(l, half, s, dst):
                for part in range(2):
                    pe.wait_ge(h_ready, 8 * l + 4 * half + 2 * s + part + 1)
                    turn(dst[:, 512 * part:], [Hn[:, s, k::KT] for k in range(4 * part, 4 * part + 4)], h_turned)

            def hT_wait(l, half, s, k):
                if k % 4 == 0:
                    pe.wait_ge((hT_ready0, hT_ready1)[s], 4 * l + 2 * half + k // 4 + 1)

            def project(l, s, n, u):
                q = (Q[0], Q[3], Q[1], Q[2])[2 * s + n % 4 // 2]
                if n >= 4:
                    pe.wait_ge(proj_kept, 16 * l + 8 * s + n - 3)
                for k in range(KT):
                    if n == 0:
                        hT_wait(l, 0, s, k)
                    mm = pe.matmul(q[:, 512 * (n % 2):512 * (n % 2) + UC], hT[:, k, P * s:P * (s + 1)], u[:, k, :],
                                   start=k == 0, stop=k == KT - 1)
                mm.then_inc(unit_used if s else proj_done, 1)

            pe.wait_ge(cs_ready, 3)
            pe.sem_inc(gu_done, 1)
            pe.sem_inc(d_done, 1)
            ada(0, 1, 0)
            pe.wait_ge(consts_loaded, 16)
            pe.wait_ge(rows_picked, 1)
            for l in range(DEPTH):
                rows_to_all(l, 1, 0, Q[2])
                if l == 0:
                    ada(0, 0, 4)
                if l:
                    pe.wait_ge(out_used, 4 * l - 1)
                rows_to_all(l, 0, 0, Q[0])
                turn_h(l, 0, 0, Q[2])
                us = []
                for n in range(8):
                    us.append(unit(8 + n))
                    project(l, 0, n, us[n])
                    if n == 3:
                        if l:
                            pe.wait_ge(out_used, 4 * l)
                        rows_to_all(l, 1, 1, Q[1])
                        rows_to_all(l, 0, 1, Q[2])
                    if n == 6:
                        turn_h(l, 0, 1, Q[1])
                for n in range(8):
                    project(l, 1, n, us[n])

                pe.wait_ge(small_loaded, SMALL * (l + 1))
                pe.wait_ge(tables_loaded, 16)
                pool_t = const("pool").rearrange("p (g n) -> p g n", g=4)
                for s in range(2):
                    pe.wait_ge(proj_kept, 16 * l + 8 + 8 * s)
                    for g in range(4):
                        r, pair = g % 2, g // 2
                        mm = pe.matmul(Q[0][64 * r:64 * r + 64, 512 * s + P * pair:512 * s + P * (pair + 1)],
                                       PR[:, s, 64 * g:64 * g + 64], pool_t[:, g, :], start=True, stop=True)
                    mm.then_inc(pool_done, 1)

                def turn_qk(s):
                    pe.wait_ge(qk_ready, 2 * l + s + 1)
                    qs = [QN[:, s, i, :, :].rearrange("p r n -> p (r n)") for i in range(3)]
                    qs += [PR[:, s, CQC + P * i:CQC + P * (i + 1)] for i in range(3)]
                    ks = [PR[:, s, CKB:CKB + P]] + [PR[:, s, CKC + P * i:CKC + P * (i + 1)] for i in range(3)]
                    if s == 1:
                        ks += [ck_b[:, :]] + [ck_c[:, P * i:P * (i + 1)] for i in range(3)]
                        pe.wait_ge(q_kept, 2 * l + 1)
                    turn(Q[1], qs, q_turned)
                    if s == 1:
                        pe.wait_ge(k_kept, 4 * l + 2)
                    turn(Q[2], ks, k_turned)

                turn_qk(0)
                ada(l, 2, 16)
                for s in range(2):
                    pe.wait_ge(pooled_kept, 2 * l + s + 1)
                    for pair in range(2):
                        mm = pe.matmul(Q[0][:, 512 * s + P * pair:512 * s + P * (pair + 1)], poolw[:, pair, :],
                                       pooled[:, s, pair, :], start=True, stop=True)
                    mm.then_inc(poolmix_done, 1)
                ada(l, 4, 20)

                def scores(u):
                    s, i = u // 6, u % 6
                    w = P * (1 + s)
                    if u >= 2:
                        pe.wait_ge(exp_done, 24 * l + 2 * (u - 2) + 2)
                    out = Q[0][:, 512 * (u % 2):512 * (u % 2) + 2 * w]
                    near = s == 1 and i >= 3
                    mm = pe.matmul(out, QT[:, s, i, :], KM[s][:, max(0, i - 2), :, :].rearrange("p r n -> p (r n)"),
                                   start=True, stop=not near)
                    if near:
                        mm = pe.matmul(out.rearrange("p (r n) -> p r n", r=2)[:, :, 0:P], const("flip"),
                                       relb[:, 2 * (i - 3):2 * (i - 3) + 2, :], start=False, stop=True)
                    mm.then_inc(score_done, 1)

                def turn_p(u):
                    s = u // 6
                    pe.wait_ge(exp_done, 24 * l + 2 * u + 2)
                    if u >= 2:
                        pe.wait_ge(p_kept, 12 * l + u - 1)
                    turn(Q[1][:, 512 * (u % 2):512 * (u % 2) + 512],
                         [PX[:, u % 2, P * n:P * (n + 1)] for n in range(2 * (1 + s))], p_turned)

                def values(u):
                    s, i = u // 6, u % 6
                    pe.wait_ge(p_kept, 12 * l + u + 1)
                    if u >= 2:
                        pe.wait_ge(o_kept, 12 * l + u - 1)
                    if i < 3:
                        vs = [PR[:, s, CVB:CVB + P], cv_b[:, :]]
                    else:
                        vs = [PR[:, s, CVC + P * (i - 3):CVC + P * (i - 2)], cv_c[:, P * (i - 3):P * (i - 2)]]
                    for r in range(2):
                        for t in range(1 + s):
                            n = r * (1 + s) + t
                            mm = pe.matmul(Q[2][:, 512 * (u % 2) + P * r:512 * (u % 2) + P * (r + 1)],
                                           PT[:, u % 2, P * n:P * (n + 1)], vs[t], start=t == 0, stop=t == s)
                    mm.then_inc(pv_done, 1)

                pe.wait_ge(q_kept, 2 * l + 1)
                pe.wait_ge(k_kept, 4 * l + 2)
                pe.wait_ge(poolmix_kept, 2 * l + 2)
                for u in range(2):
                    scores(u)
                turn_qk(1)
                pe.wait_ge(q_kept, 2 * l + 2)
                pe.wait_ge(k_kept, 4 * l + 4)
                for u in range(1, 14):
                    if 2 <= u < 12:
                        scores(u)
                    if u <= 12:
                        turn_p(u - 1)
                    if u >= 2:
                        values(u - 2)
                    if u == 4:
                        pe.wait_ge(row_ready, 6 * l + 3)
                        ada(l, 3, 24)
                for s in range(2):
                    pe.wait_ge(o_kept, 12 * l + 6 + 6 * s)
                    turn(Q[s], [ON[:, s, 2 * i:2 * i + 2, :].rearrange("p h n -> p (h n)") for i in range(6)], o_turned)
                pe.wait_ge(row_ready, 6 * l + 5)
                for s in range(2):
                    rows_to_all(l, 2, s, Q[2 + s])

                us = [unit(28 + n) for n in range(4)]
                for s in range(2):
                    if s == 1:
                        pe.wait_ge(gate_ready, 4 * l + 2)
                        rows_to_all(l, 4, 0, Q[2])
                        rows_to_all(l, 3, 0, Q[3])
                    pe.wait_ge((mix_ready0, mix_ready1)[s], l + 1)
                    for n in range(4):
                        for k in range(KT):
                            mm = pe.matmul(Q[s][:, UC * n:UC * (n + 1)], mixT[:, k, P * s:P * (s + 1)], us[n][:, k, :],
                                           start=k == 0, stop=k == KT - 1)
                        mm.then_inc(unit_used if s else out_done, 1)

                turn_h(l, 1, 0, Q[2])
                pe.wait_ge(router_loaded, 64 * (l + 1))

                def route(s, out):
                    for k in range(KT):
                        hT_wait(l, 1, s, k)
                        mm = pe.matmul(out, hT[:, k, P * s:P * (s + 1)], rw[:, k, :], start=k == 0, stop=k == KT - 1)
                    mm.then_inc(logits_done, 1)

                pe.wait_ge(out_used, 4 * l + 1)
                rows_to_all(l, 4, 1, Q[0])
                pe.wait_ge(h_ready, 8 * l + 6)
                ada(l, 5, 32)
                pe.wait_ge(out_used, 4 * l + 2)
                rows_to_all(l, 3, 1, Q[1])
                turn_h(l, 1, 1, Q[0])
                route(0, Q[3][:, 0:NG + NE])
                route(1, Q[2][:, 0:NG + NE])
                pe.wait_ge(chosen, l + 1)
                all16 = ones16[:, :].broadcast_to([P, P])
                pe.matmul(Q[1][:, 0:NE], before16[:, :], M[:, 0, :], start=True, stop=True)
                pe.matmul(Q[1][:, 64:64 + NE], all16, M[:, 0, :], start=True, stop=False)
                pe.matmul(Q[1][:, 64:64 + NE], all16, M[:, 1, :], start=False, stop=True)
                pe.matmul(Q[1][:, 512:512 + NE], before16[:, :], M[:, 1, :], start=True, stop=False)
                pe.matmul(Q[1][:, 512:512 + NE], all16, M[:, 0, :], start=False, stop=True).then_inc(counted, 1)

                def gather(k, to, lo, counts):
                    for s in range(2):
                        pe.wait_ge(pick_ready, 4 * l + (2 if lo else 0) + s + 1)
                        mm = pe.matmul(to, Hn[:, s, k::KT], pick[:, s, lo:lo + HALF], start=s == 0, stop=s == 1)
                    if counts:
                        mm.then_inc(gathered, 1)

                for k in range(KT):
                    gather(k, Q[k // 2][:, 512 * (k % 2):512 * (k % 2) + HALF], 0, True)
                pe.wait_ge(sorted_kept, 13 * l + 9)

                def gather_rest():
                    for k in range(KT):
                        gather(k, Q[2 + k // 4][:, HALF * (k % 4):HALF * (k % 4 + 1)], HALF, k % 2 == 1)

                def weights_and_gate():
                    pe.wait_ge(sorted_kept, 13 * l + 13)
                    rows_to_all(l, 5, 0, Q[3])
                    pe.wait_ge(pickw_ready, l + 1)
                    for i in range(4):
                        for s in range(2):
                            t = pe.transpose(Q[2][:, 256 * i + P * s:256 * i + P * (s + 1)],
                                             pickw[:, s, P * i:P * (i + 1)], ident)
                    t.then_inc(w_turned, 1)

                pe.wait_ge(tab_ready, l + 1)

                def fold(g):
                    pe.wait_ge(a2_ready, 4 * (g + 1))
                    pe.wait_ge(at_kept, g + l + 1)
                    pe.matmul(ATp, A2[:, :], const("fold"), start=True, stop=True).then_inc(s_done, 1)

                def turn_y(g):
                    pe.wait_ge(y_kept, g + l + 1)
                    pe.wait_ge(yt_kept, g + 2 * l + 1)
                    for h in range(2):
                        t = pe.transpose(YTp[:, P * h:P * (h + 1)], Yb[:, P * h:P * (h + 1)], ident)
                    t.then_inc(yt_done, 1)

                def down(g, i):
                    pe.wait_ge(at_kept, g + l + 2)
                    wd = slot(3 * i + 2).rearrange("p (q n) -> p q n", q=2)
                    for q in range(2):
                        for j in range(4):
                            mm = pe.matmul(Yp[32 * j:32 * j + 32, :], AT[:, BLK * q:BLK * (q + 1)],
                                           wd[:, q, UC * j:UC * (j + 1)], start=q == 0, stop=q == 1)
                    mm.then_inc(d_done, 1)

                def expert(e, i, loads, first, second, ahead):
                    wgu = ring[:, 3 * i * UNIT:(3 * i + 2) * UNIT].rearrange("p (w k n) -> p w k n", w=2, k=KT)
                    before = (i - 1) % ROUND if not first else i

                    def products(g, head):
                        if head:
                            pe.wait_ge(slot_loaded[3 * i], 16 * loads)
                            pe.wait_ge(slot_loaded[3 * i + 1], 16 * loads)
                        pe.wait_ge(hb_ready, g + 1)
                        for k in range(KT):
                            for j in range(4):
                                mm = pe.matmul(GU[32 * j:32 * j + 32, :], hb[:, k, :], wgu[:, :, k, HD * j:HD * (j + 1)],
                                               start=k == 0, stop=k == KT - 1)
                        mm.then_inc(gu_done, 1)

                    def down_before(g, head):
                        if head and second:
                            return
                        if head and first:
                            pe.wait_ge(slot_loaded[3 * i + 2], 16 * loads)
                        elif head:
                            pe.wait_ge(slot_loaded[3 * before + 2], 16 * (loads - (1 if i == 0 else 0)))
                        else:
                            pe.wait_ge(slot_loaded[3 * i + 2], 16 * loads)
                        down(g, before if head else i)

                    def body(g, _, head):
                        if not (head and second):
                            fold(g)
                        turn_y(g)
                        if not ahead:
                            down_before(g, head)
                        products(g, head)
                        if ahead:
                            down_before(g, head)

                    blocks_of_expert(pe, e, body, with_start=False)

                per = MIXER_UNITS // SLOTS + NE // ROUND
                done = per * l + MIXER_UNITS // SLOTS
                for i in range(ROUND):
                    expert(i, i, done + 1, i == 0, i == 1, False)
                    if i == 0:
                        last = entry(pe, 2, 1, 1, MAXB)
                        fold(last)
                        down(last, 0)
                        gather_rest()
                    if i == 1:
                        weights_and_gate()
                    if i == 2:
                        pe.wait_ge(gate_ready, 4 * l + 3)
                        rows_to_all(l, 5, 1, Q[3])
                for lo, hi, ahead in ((1, LAST_ROUND, False), (LAST_ROUND, LAST_ROUND + 1, True)):
                    with pe.Fori(lo, hi) as turn_no:
                        for i in range(ROUND):
                            expert(turn_no * ROUND + i, i, turn_no + (done + 1), False, False, ahead)
                total = entry(pe, 2, NE, 1, MAXB)
                fold(total)
                turn_y(total)
                pe.wait_ge(slot_loaded[SLOTS - 1], 16 * (per * (l + 1)))
                down(total, ROUND - 1)
                turn_y(total + 1)
                for m in range(SLOTS):
                    used[m] = per * (l + 1)

                pe.wait_ge(yt_kept, total + 2 * l + 3)
                pe.wait_ge(gate_ready, 4 * l + 4)
                pe.wait_ge(w_kept, l + 1)

                def combine(s, lo, hi, i):
                    mm = pe.matmul(Q[s][:, lo:hi], CT[:, i, P * s:P * (s + 1)], yS[:, i, lo:hi], start=i == 0, stop=i == 3)
                    if i == 3:
                        mm.then_inc(comb_done, 1)

                for i in range(6):
                    if i < 4:
                        if i >= 2:
                            pe.wait_ge(ys_kept, 4 * l + i - 1)
                        turn(Q[2 + i % 2], [yST[:, k, P * i:P * (i + 1)] for k in range(KT)], ys_turned)
                    if i >= 2:
                        pe.wait_ge(ys_kept, 4 * l + i - 1)
                        for lo in (0, 512):
                            combine(0, lo, lo + 512, i - 2)
                if l + 1 < DEPTH:
                    for n, v in enumerate(ROW_ORDER[:2]):
                        ada(l + 1, v, 4 * n)
                for lo, hi in CHUNKS:
                    for i in range(4):
                        combine(1, lo, hi, i)

        @block.scalar
        def _(act):
            steps = [0]

            def after(ins):
                steps[0] += 1
                ins.then_inc(act_step, 1)
                act.wait_ge(act_step, steps[0])

            act.wait_ge(cs_cleared, 1)
            act.wait_ge(c_loaded, 32)
            for q in range(3):
                act.activation(CS[:, :, 2 * q:2 * q + 2].rearrange("p k s -> p s k"), cvec[:, :, :], ACT.Silu)\
                   .then_inc(cs_ready, 1)
            act.sem_inc(at_kept, 1)
            for l in range(DEPTH):
                def keep_h(half, s):
                    src = (Q[2], (Q[1], Q[0])[half])[s]
                    for part in range(2):
                        act.wait_ge(h_turned, 8 * l + 4 * half + 2 * s + part + 1)
                        act.copy(hT[:, 4 * part:4 * part + 4, P * s:P * (s + 1)],
                                 src[:, 512 * part:512 * part + 512].rearrange("p (k n) -> p k n", k=4))\
                           .then_inc((hT_ready0, hT_ready1)[s], 1)

                keep_h(0, 0)
                for s in range(2):
                    for n in range(8):
                        if s == 0:
                            act.wait_ge(proj_done, 8 * l + n + 1)
                        else:
                            act.wait_ge(unit_used, MIXER_UNITS * l + 8 + n + 1)
                        q = (Q[0], Q[3], Q[1], Q[2])[2 * s + n % 4 // 2]
                        act.copy(PR[:, s, UC * n:UC * (n + 1)], q[:, 512 * (n % 2):512 * (n % 2) + UC])\
                           .then_inc(proj_kept, 1)
                        if s == 0 and n == 6:
                            keep_h(0, 1)
                for s in range(2):
                    act.wait_ge(pool_done, 2 * l + s + 1)
                    act.copy(pooled[:, s, :, :], Q[0][:, 512 * s:512 * s + 2 * P].rearrange("p (a n) -> p a n", a=2))\
                       .then_inc(pooled_kept, 1)
                act.wait_ge(small_loaded, SMALL * (l + 1))
                def keep_q(s):
                    act.wait_ge(q_turned, 2 * l + s + 1)
                    act.activation(QT[:, s, :, :], Q[1][:, 0:6 * P].rearrange("p (i n) -> p i n", i=6), ACT.Copy,
                                   scale=HD ** -0.5).then_inc(q_kept, 1)

                def keep_k(s, r):
                    act.wait_ge(k_turned, 2 * l + s + 1)
                    act.copy(*key_rows(s, r)).then_inc(k_kept, 1)

                keep_q(0)
                keep_k(0, 0)
                keep_k(0, 1)
                for s in range(2):
                    act.wait_ge(poolmix_done, 2 * l + s + 1)
                    for pair in range(2):
                        ins = act.activation(mixT[:, pair, P * s:P * (s + 1)],
                                             Q[0][:, 512 * s + P * pair:512 * s + P * (pair + 1)], ACT.Copy,
                                             scale=pools[:, pair:pair + 1])
                        if pair == 0:
                            after(ins)
                    ins.then_inc(poolmix_kept, 1)

                def exps(u):
                    s, i = u // 6, u % 6
                    w = P * (1 + s)
                    act.wait_ge(max_ready, 12 * l + u + 1)
                    if u >= 2:
                        act.wait_ge(p_turned, 12 * l + u - 1)
                    for r in range(2):
                        src = SX[:, u % 2, w * r:w * (r + 1)] if s and i >= 3 else \
                            Q[0][:, 512 * (u % 2) + w * r:512 * (u % 2) + w * (r + 1)]
                        act.activation(PX[:, u % 2, w * r:w * (r + 1)], src, ACT.Exp, bias=nmx[:, 2 * u + r:2 * u + r + 1],
                                       accum_out=sums[:, 2 * u + r:2 * u + r + 1]).then_inc(exp_done, 1)

                def keep_p(u):
                    w = 256 * (1 + u // 6)
                    act.wait_ge(p_turned, 12 * l + u + 1)
                    if u >= 2:
                        act.wait_ge(pv_done, 12 * l + u - 1)
                    act.copy(PT[:, u % 2, 0:w], Q[1][:, 512 * (u % 2):512 * (u % 2) + w]).then_inc(p_kept, 1)

                for u in range(2):
                    exps(u)
                keep_q(1)
                keep_k(1, 1)
                for u in range(1, 13):
                    if u < 7 and 2 <= u:
                        exps(u)
                    keep_p(u - 1)
                    if 7 <= u < 12:
                        exps(u)
                act.wait_ge(o_turned, 2 * l + 1)
                act.copy(mixT[:, 2:8, 0:P], Q[0][:, 0:6 * P].rearrange("p (i n) -> p i n", i=6)).then_inc(mix_ready0, 1)

                def keep_gate(first_bc, s, src):
                    act.wait_ge(bc_done, 12 * l + first_bc + s + 1)
                    act.copy(GB[:, s, :], src[:, :]).then_inc(gate_ready, 1)

                for s in range(2):
                    keep_gate(4, s, Q[2 + s])
                keep_h(1, 0)
                keep_h(1, 1)
                act.wait_ge(group_shift, l + 1)
                act.activation(gb[:, :, :], ga[:, :, :], ACT.Exp).then_inc(group_exp, 1)
                act.wait_ge(pair_diff, l + 1)
                act.activation(sc[:, 6:8], sc[:, 4:6], ACT.Exp).then_inc(pair_exp, 1)
                act.wait_ge(kv_stored, 64 * (l + 1))
                for k in range(0, KT, 2):
                    act.wait_ge(gathered, 12 * l + k + 1)
                    act.copy(hS[:, k, 0:HALF], Q[k // 2][:, 0:HALF]).then_inc(sorted_kept, 1)

                act.preload_act_table(ACT.Silu)
                act.wait_ge(tab_ready, l + 1)

                def keep_at(g):
                    act.wait_ge(s_done, g + l + 1)
                    act.wait_ge(d_done, g + l + 1)
                    act.copy(AT[:, :], ATp).then_inc(at_kept, 1)

                def keep_y(g):
                    act.wait_ge(d_done, g + l + 2)
                    act.wait_ge(yt_done, g + 2 * l + 1)
                    act.copy(Yb[:, :], Yp).then_inc(y_kept, 1)

                def body(g, ahead):
                    keep_at(g)
                    if not ahead:
                        keep_y(g)
                    act.wait_ge(gu_done, g + 2)
                    act.wait_ge(a2_ready, 4 * (g + 1))
                    act.activation(SG[:, :], GU[:, 0:HD], ACT.Silu).then_inc(sg_ready, 1)
                    if ahead:
                        keep_y(g)

                def expert(e, ahead):
                    blocks_of_expert(act, e, lambda g, _, head: body(g, ahead), with_start=False)

                expert(0, False)
                expert(1, False)
                keep_gate(10, 0, Q[3])
                act.wait_ge(w_turned, l + 1)
                act.copy(CT[:, :, :].rearrange("p i n -> p (i n)"), Q[2][:, :]).then_inc(w_kept, 1)
                expert(2, False)
                keep_gate(10, 1, Q[3])
                expert(3, False)
                for lo, hi, ahead in ((ROUND, ROUND * LAST_ROUND, False), (ROUND * LAST_ROUND, NE, True)):
                    with act.Fori(lo, hi) as e:
                        expert(e, ahead)
                total = entry(act, 2, NE, 1, MAXB)
                keep_at(total)
                keep_y(total)

                for i in (0, 2):
                    act.wait_ge(ys_turned, 4 * l + i + 1)
                    if l or i:
                        act.wait_ge(ys_kept, 4 * l + i)
                    act.copy(yS[:, i, :], Q[2][:, :]).then_inc(ys_kept, 1)

        @block.vector
        def _(v):
            steps = [0]

            def after(ins):
                steps[0] += 1
                ins.then_inc(dve_step, 1)
                v.wait_ge(dve_step, steps[0])

            after(v.memset(CS[:, :, :], 0.0))
            v.sem_inc(cs_cleared, 1)
            after(v.memset(bias_rows[:, :, :], 0.0))
            v.sem_inc(rows_cleared, 1)
            for t in (KM[0][:, :, :, :], KM[1][:, :, :, :], poolw[:, :, :], A2[:, :], Yb[:, :],
                      ln1_rows[:, :, :]):
                after(v.memset(t, 0.0))
            v.sem_inc(cleared, 1)
            v.sem_inc(a2_ready, 4)
            v.sem_inc(y_kept, 1)
            v.sem_inc(yt_kept, 1)
            run_1 = v.alloc_register("run_1")
            run_2 = v.alloc_register("run_2")

            def keep_row(l, r):
                n = ROW_ORDER.index(r)
                v.wait_ge(unit_used, MIXER_UNITS * l + (4, 8, 20, 24, 28, 36)[n])
                if r == ROW_ORDER[0]:
                    v.wait_ge(bias_loaded, 96 * (l + 1))
                row = Q[3][:, 512 * (n % 2):512 * (n % 2) + UC]
                after(v.tensor_tensor(row_f, row, bias_rows[:, r, :], ALU.add))
                if r == 1:
                    after(v.tensor_scalar(row_f, row_f, 1.0, None, ALU.add))
                if r == 4:
                    after(v.scalar_tensor_tensor(out=row_rest, in0=row_f, scalar=1.0, in1=ln1_rows[:, 1, :], op0=ALU.add,
                                                 op1=ALU.mult))
                    after(v.tensor_tensor(bias_rows[:, 3, :], bias_rows[:, 3, :], row_rest, ALU.add))
                    after(v.scalar_tensor_tensor(out=row_f, in0=row_f, scalar=1.0, in1=ln1_rows[:, 0, :], op0=ALU.add,
                                                 op1=ALU.mult))
                after(v.tensor_copy(part16[:, :], row_f))
                after(v.scalar_tensor_tensor(out=row_rest, in0=part16[:, :], scalar=const("part")[:, 0:1], in1=row_f,
                                             op0=ALU.mult, op1=ALU.add))
                after(v.tensor_copy(part16[:, :], row_rest))
                v.scalar_tensor_tensor(out=R[:, r, :], in0=part16[:, :], scalar=const("part")[:, 1:2], in1=row_rest,
                                       op0=ALU.mult, op1=ALU.add).then_inc(row_ready, 1)
                v.wait_ge(row_ready, 6 * l + n + 1)

            def modulate(l, half, s):
                G, B = ((Q[2], Q[0]), (Q[1], Q[2]))[s] if half == 0 else ((Q[2], Q[3]), (Q[0], Q[1]))[s]

                def part(t, n):
                    return t.rearrange("p (c k) -> p c k", k=KT)[:, :, 4 * n:4 * n + 4]

                v.wait_ge(bc_done, 12 * l + 6 * half + 2 * s + 1)
                after(v.tensor_tensor(Hn[:, s, :], G[:, :], X[:, s, :], ALU.mult))
                v.wait_ge(bc_done, 12 * l + 6 * half + 2 * s + 2)
                for n in range(2):
                    v.tensor_tensor(part(Hn[:, s, :], n), part(B[:, :], n), part(Hn[:, s, :], n), ALU.add).then_inc(h_ready, 1)

            def join(l, which, s, c):
                lo, hi = CHUNKS[c]
                if which == 1:
                    v.wait_ge(comb_done, 4 * l + 2 * s + c + 1)
                elif s == 0:
                    v.wait_ge(out_done, 4 * l + hi // UC)
                else:
                    v.wait_ge(unit_used, MIXER_UNITS * l + 28 + hi // UC)
                if c == 0:
                    v.wait_ge(gate_ready, 4 * l + 2 * which + 2)
                after(v.tensor_tensor(GB[:, s, lo:hi], Q[s][:, lo:hi], GB[:, s, lo:hi], ALU.mult))
                after(v.scalar_tensor_tensor(out=X[:, s, lo:hi], in0=X[:, s, lo:hi], scalar=ALPHA,
                                             in1=GB[:, s, lo:hi], op0=ALU.mult, op1=ALU.add))
                if c == len(CHUNKS) - 1:
                    v.sem_inc(out_used, 1)
                after(v.bn_stats(st[:, 40 + 6 * c:46 + 6 * c], X[:, s, lo:hi]))

            def mean_and_variance():
                after(v.bn_aggr(st[:, 12:14], st[:, 40:40 + 6 * len(CHUNKS)]))
                after(v.tensor_scalar(st[:, 15:16], st[:, 13:14], EPS, None, ALU.add))
                v.sem_inc(var_ready, 1)

            def norm(l, which, s):
                v.wait_ge(rstd_ready, 6 * l + 2 + 2 * which + s + 1)
                after(v.tensor_scalar(X[:, s, :], X[:, s, :], st[:, 12:13], st[:, 14:15], ALU.subtract, ALU.mult))

            def normed(l, which, s):
                for c in range(len(CHUNKS)):
                    join(l, which, s, c)
                mean_and_variance()
                norm(l, which, s)

            def weigh(s, W, n, cols=slice(0, D)):
                after(v.tensor_tensor(X[:, s, cols], X[:, s, cols], W[:, n, cols], (ALU.mult, ALU.add)[n]))
                if n == 1:
                    v.sem_inc(x_ready, 1)

            def weighed(l, which, s, W):
                v.wait_ge(ln_loaded, 32 * (2 * l + which + 1))
                for n in range(2):
                    weigh(s, W, n)

            def first_of_max(out, x, top, rank, tmp, others=False):
                sh = list(x.shape)
                after(v.tensor_reduce(top, x, AX.X, ALU.max))
                after(v.tensor_tensor(tmp, x, top.unsqueeze(2).broadcast_to(sh), ALU.is_equal))
                after(v.tensor_tensor(tmp, tmp, rank.unsqueeze(1).broadcast_to(sh), ALU.mult))
                after(v.tensor_reduce(sc[:, 30:32], tmp, AX.X, ALU.max))
                after(v.tensor_tensor(out, tmp, sc[:, 30:32].unsqueeze(2).broadcast_to(sh),
                                      ALU.subtract if others else ALU.is_equal))

            v.wait_ge(consts_loaded, 16)
            v.tensor_copy(rows16[:, :], const("rows")).then_inc(rows_picked, 1)
            for r in ROW_ORDER[:2]:
                keep_row(0, r)
            v.wait_ge(x0_loaded, 16)
            for l in range(DEPTH):
                modulate(l, 0, 0)
                if l:
                    normed(l - 1, 1, 1)
                    weighed(l - 1, 1, 1, LN2)
                else:
                    v.wait_ge(x1_loaded, 16)
                modulate(l, 0, 1)
                v.wait_ge(tables_loaded, 16)
                if l == 0:
                    after(v.tensor_copy(before16[:, :], const("before")))
                    after(v.tensor_copy(ones16[:, :], const("ones")[:, 0:1]))
                v.wait_ge(small_loaded, SMALL * (l + 1))
                for s in range(2):
                    v.wait_ge(proj_kept, 16 * l + 8 + 8 * s)
                    qk = PR[:, s, CQB:CVB].rearrange("p (h n) -> p h n", n=HD)
                    t1 = T1.rearrange("p (h n) -> p h n", n=HD)
                    after(v.tensor_tensor(t1, qk, qk, ALU.mult))
                    after(v.tensor_reduce(st[:, 16:24], t1, AX.X, ALU.add))
                    after(v.tensor_scalar(st[:, 24:32], st[:, 16:24], 1.0 / HD, EPS, ALU.mult, ALU.add))
                    v.sem_inc(var_ready, 1)
                    v.wait_ge(rstd_ready, 6 * l + s + 1)
                    after(v.tensor_tensor(qk, qk, st[:, 32:40].unsqueeze(2).broadcast_to([P, 8, HD]), ALU.mult))
                    q6 = qk[:, 0:6, :].rearrange("p (r i) n -> p r i n", r=2)
                    qn = QN[:, s, :, :, :].rearrange("p i r n -> p r i n")
                    w6 = qk_w[:, 0, :].unsqueeze(1).unsqueeze(1).broadcast_to([P, 2, 3, HD])
                    after(v.tensor_tensor(q6 if s else qn, q6, w6, ALU.mult))
                    after(v.tensor_tensor(qk[:, 6:8, :], qk[:, 6:8, :],
                                          qk_w[:, 1, :].unsqueeze(1).broadcast_to([P, 2, HD]), ALU.mult))
                    if s == 1:
                        flat = PR[:, s, CQB:CVB].rearrange("p (h a b n) -> p h a b n", a=2, b=2, n=HD // 4)
                        tf = T1.rearrange("p (h a b n) -> p h a b n", a=2, b=2, n=HD // 4)
                        sn = const("sin").rearrange("p (a b n) -> p a b n", a=2, b=2)
                        for a in range(2):
                            for b in range(2):
                                after(v.tensor_tensor(tf[:, :, a, b, :], flat[:, :, a, 1 - b, :],
                                                      sn[:, a, b, :].unsqueeze(1).broadcast_to([P, 8, HD // 4]), ALU.mult))
                        after(v.tensor_tensor(qk, qk, const("cos").unsqueeze(1).broadcast_to([P, 8, HD]), ALU.mult))
                        after(v.tensor_tensor(qn, q6, t1[:, 0:6, :].rearrange("p (r i) n -> p r i n", r=2), ALU.add))
                        after(v.tensor_tensor(qk[:, 6:8, :], qk[:, 6:8, :], t1[:, 6:8, :], ALU.add))
                    v.sem_inc(qk_ready, 1)

                def row_max(u):
                    s, i = u // 6, u % 6
                    w = P * (1 + s)
                    v.wait_ge(score_done, 12 * l + u + 1)
                    src = Q[0][:, 512 * (u % 2):512 * (u % 2) + 2 * w].rearrange("p (r n) -> p r n", r=2)
                    if s and i >= 3:
                        to = SX[:, u % 2, :].rearrange("p (r n) -> p r n", r=2)
                        v.wait_ge(exp_done, 24 * l + 2 * (u - 2) + 2)
                        after(v.tensor_tensor(to[:, :, 0:P], src[:, :, 0:P],
                                              const("mask").unsqueeze(1).broadcast_to([P, 2, P]), ALU.add))
                        after(v.tensor_copy(to[:, :, P:2 * P], src[:, :, P:2 * P]))
                        src = to
                    after(v.tensor_reduce(rsum[:, 2 * u:2 * u + 2], src, AX.X, ALU.max))
                    v.tensor_scalar(nmx[:, 2 * u:2 * u + 2], rsum[:, 2 * u:2 * u + 2], -1.0, None, ALU.mult)\
                     .then_inc(max_ready, 1)

                def keep_o(u):
                    s, i = u // 6, u % 6
                    v.wait_ge(max_ready, 12 * l + u + 1)
                    v.wait_ge(exp_done, 24 * l + 2 * u + 2)
                    after(v.reciprocal(rsum[:, 2 * u:2 * u + 2], sums[:, 2 * u:2 * u + 2]))
                    v.wait_ge(pv_done, 12 * l + u + 1)
                    dst = ON[:, s, i:i + 4:3, :] if i < 3 else ON[:, s, 2 * i:2 * i + 2, :]
                    o = Q[2][:, 512 * (u % 2):512 * (u % 2) + 2 * P].rearrange("p (a n) -> p a n", n=HD)[:, 0:4:3, :]
                    v.tensor_tensor(dst, o, rsum[:, 2 * u:2 * u + 2].unsqueeze(2).broadcast_to([P, 2, HD]), ALU.mult)\
                     .then_inc(o_kept, 1)

                for u in range(2):
                    row_max(u)
                v.wait_ge(k_turned, 2 * l + 2)
                v.tensor_copy(*key_rows(1, 0)).then_inc(k_kept, 1)
                for u in range(1, 14):
                    if 2 <= u < 12:
                        row_max(u)
                    if u >= 2:
                        keep_o(u - 2)
                    if u in (2, 4, 7):
                        keep_row(l, {2: 2, 4: 4, 7: 3}[u])
                v.wait_ge(o_turned, 2 * l + 2)
                v.tensor_copy(mixT[:, 2:8, P:2 * P], Q[1][:, 0:6 * P].rearrange("p (i n) -> p i n", i=6))\
                 .then_inc(mix_ready1, 1)

                for s in range(2):
                    normed(l, 0, s)
                    modulate(l, 1, s)
                    weighed(l, 0, s, LN1)

                keep_row(l, 5)

                v.wait_ge(logits_done, 2 * l + 2)
                v.wait_ge(router_loaded, 64 * (l + 1))
                for s in range(2):
                    after(v.tensor_tensor(LG[:, s, :], Q[3 - s][:, 0:NG + NE], rb[:, :], ALU.add))
                gmax = sc[:, 0:2]
                first_of_max(gb[:, :, :], LG[:, :, 0:NG], gmax, const("rank_g"), ga[:, :, :], others=True)
                after(v.scalar_tensor_tensor(out=LE[:, :, :].rearrange("p s (g e) -> p s g e", g=NG),
                                             in0=gb[:, :, :].unsqueeze(3).broadcast_to([P, 2, NG, NE // NG]), scalar=BIG,
                                             in1=LG[:, :, NG:].rearrange("p s (g e) -> p s g e", g=NG),
                                             op0=ALU.mult, op1=ALU.add))
                first_of_max(OH[0], LE[:, :, :], sc[:, 2:4], const("rank_e"), ea[:, :, :])
                after(v.scalar_tensor_tensor(out=LE[:, :, :], in0=OH[0], scalar=-2 * BIG, in1=LE[:, :, :],
                                             op0=ALU.mult, op1=ALU.add))
                first_of_max(OH[1], LE[:, :, :], sc[:, 8:10], const("rank_e"), ea[:, :, :])
                after(v.tensor_tensor(M[:, :, :], OH[0], OH[1], ALU.add))
                v.sem_inc(chosen, 1)
                after(v.tensor_tensor(ga[:, :, :], LG[:, :, 0:NG], gmax.unsqueeze(2).broadcast_to([P, 2, NG]),
                                      ALU.subtract))
                v.sem_inc(group_shift, 1)
                after(v.tensor_tensor(sc[:, 4:6], sc[:, 8:10], sc[:, 2:4], ALU.subtract))
                v.sem_inc(pair_diff, 1)
                v.wait_ge(counted, l + 1)
                count = Q[1][:, 64:64 + NE]
                after(v.tensor_tensor_scan(incl[:, :], const("ones")[:, 0:NE], count, 0.0, ALU.mult, ALU.add))
                after(v.tensor_tensor(off[:, :], incl[:, :], count, ALU.subtract))
                after(v.tensor_tensor(OP[:, :, :], Q[1][:, :].rearrange("p (s n) -> p s n", s=2)[:, :, 0:NE],
                                      off[:, :].unsqueeze(1).broadcast_to([P, 2, NE]), ALU.add))
                after(v.tensor_tensor(place, OH2[:, :, :, :], OP[:, :, :].unsqueeze(1).broadcast_to([P, 2, 2, NE]), ALU.mult))
                after(v.tensor_reduce(sc[:, 18:22].rearrange("p (a s) -> p a s", a=2), place, AX.X, ALU.add))
                for lo in (0, HALF):
                    for s in range(2):
                        p0, p1 = sc[:, 18 + s:19 + s], sc[:, 20 + s:21 + s]
                        to, place_no = pick[:, s, lo:lo + HALF], const("iota")[:, lo:lo + HALF]
                        after(v.tensor_scalar(to, place_no, p0, None, ALU.is_equal))
                        after(v.scalar_tensor_tensor(out=to, in0=place_no, scalar=p1, in1=to, op0=ALU.is_equal,
                                                     op1=ALU.add))
                        v.sem_inc(pick_ready, 1)
                after(v.tensor_tensor(cnt[0:1, :], incl[0:1, :], off[0:1, :], ALU.subtract))
                after(v.tensor_copy(tabf[0:1, 0, 0:NE], off[0:1, :]))
                after(v.tensor_tensor(cmp8[:, :, :], cnt[0:1, :].unsqueeze(2).broadcast_to([1, NE, 8]),
                                      const("steps")[0:1, :].unsqueeze(1).broadcast_to([1, NE, 8]), ALU.is_gt))
                after(v.tensor_reduce(tabf[0:1, 1, 0:NE], cmp8[:, :, :], AX.X, ALU.add))
                if l == 0:
                    after(v.memset(tabf[0:1, 2, 0:1], 0.0))
                    after(v.memset(tabf[0:1, 0:2, NE:NE + 1], 0.0))
                else:
                    after(v.tensor_copy(tabf[0:1, 2, 0:1], tabf[0:1, 2, NE:NE + 1]))
                after(v.tensor_tensor_scan(tabf[0:1, 2, 1:NE + 1], const("ones")[0:1, 0:NE], tabf[0:1, 1, 0:NE],
                                           tabf[0:1, 2, 0:1], ALU.mult, ALU.add))
                after(v.tensor_copy(tab[:, :, :], tabf[0:1, 0:3, :]))
                v.sem_inc(tab_ready, 1)
                v.wait_ge(kv_stored, 64 * (l + 1))
                v.memset(hS[:, :, PAIRS:SORTED], 0.0).then_inc(sorted_kept, 1)
                for k in range(1, KT, 2):
                    v.wait_ge(gathered, 12 * l + k + 1)
                    v.tensor_copy(hS[:, k, 0:HALF], Q[k // 2][:, 512:512 + HALF]).then_inc(sorted_kept, 1)

                def keep_yt(g):
                    to = v.snap(run_2, min_val=0, max_val=PAIRS)
                    v.wait_ge(yt_done, g + 2 * l + 1)
                    v.wait_ge(yt_kept, g + 2 * l + 1)
                    v.tensor_copy(yST.rearrange("p (j h) n -> p h j n", h=2)[:, :, :, bass.ds(to, BLK)],
                                  YTp.rearrange("p (h j n) -> p h j n", h=2, j=4)).then_inc(yt_kept, 1)

                def body(g, start, head):
                    keep_yt(g)
                    v.wait_ge(sg_ready, g + 1)
                    v.wait_ge(s_done, g + l + 1)
                    for j in range(4):
                        rows = slice(32 * j, 32 * j + 32)
                        v.tensor_tensor(A2[rows, HD * (j % 2):HD * (j % 2) + HD], GU[rows, HD:2 * HD], SG[rows, :],
                                        ALU.mult).then_inc(a2_ready, 1)
                    v.reg_mov(run_2, run_1)
                    v.reg_mov(run_1, start)

                v.reg_mov(run_1, HALF)
                v.reg_mov(run_2, HALF)
                blocks_of_expert(v, 0, body)
                v.wait_ge(group_exp, l + 1)
                after(v.tensor_reduce(sc[:, 10:12], gb[:, :, :], AX.X, ALU.add))
                v.wait_ge(pair_exp, l + 1)
                after(v.scalar_tensor_tensor(out=sc[:, 12:14], in0=sc[:, 6:8], scalar=1.0, in1=sc[:, 10:12], op0=ALU.add,
                                             op1=ALU.mult))
                after(v.reciprocal(sc[:, 14:16], sc[:, 12:14]))
                after(v.tensor_tensor(sc[:, 16:18], sc[:, 14:16], sc[:, 6:8], ALU.mult))
                for s in range(2):
                    p0, p1 = sc[:, 18 + s:19 + s], sc[:, 20 + s:21 + s]
                    after(v.tensor_scalar(pickw[:, s, :], const("iota"), p0, sc[:, 14 + s:15 + s], ALU.is_equal, ALU.mult))
                    after(v.tensor_scalar(tmpw, const("iota"), p1, sc[:, 16 + s:17 + s], ALU.is_equal, ALU.mult))
                    after(v.tensor_tensor(pickw[:, s, :], pickw[:, s, :], tmpw, ALU.add))
                v.sem_inc(pickw_ready, 1)
                for n in range(4):
                    v.wait_ge(gathered, 12 * l + 8 + n + 1)
                    v.tensor_copy(*second_half(n)).then_inc(sorted_kept, 1)
                with v.Fori(1, NE) as e:
                    blocks_of_expert(v, e, body)
                total = entry(v, 2, NE, 1, MAXB)
                keep_yt(total)
                v.reg_mov(run_2, run_1)
                keep_yt(total + 1)

                for i in (1, 3):
                    v.wait_ge(ys_turned, 4 * l + i + 1)
                    v.wait_ge(ys_kept, 4 * l + i)
                    v.tensor_copy(yS[:, i, :], Q[3][:, :]).then_inc(ys_kept, 1)
                if l + 1 < DEPTH:
                    normed(l, 1, 0)
                    weighed(l, 1, 0, LN2)
                    for r in ROW_ORDER[:2]:
                        keep_row(l + 1, r)
                else:
                    v.wait_ge(ln_loaded, 32 * (2 * l + 2))
                    join(l, 1, 0, 0)
                    join(l, 1, 0, 1)
                    mean_and_variance()
                    join(l, 1, 1, 0)
                    norm(l, 1, 0)
                    weigh(0, LN2, 0)
                    join(l, 1, 1, 1)
                    mean_and_variance()
                    weigh(0, LN2, 1)
                    norm(l, 1, 1)
                    for cols in (slice(0, D // 2), slice(D // 2, D)):
                        for n in range(2):
                            weigh(1, LN2, n, cols)

        @block.gpsimd
        def _(po):
            def rstd(n, dst, var):
                po.wait_ge(var_ready, n + 1)
                po.tensor_tensor(dst, var, const("power")[:, 0:dst.shape[1]], ALU.pow).then_inc(rstd_ready, 1)

            po.wait_ge(cleared, 1)
            po.wait_ge(tables_loaded, 16)
            for l in range(DEPTH):
                for s in range(2):
                    rstd(6 * l + s, st[:, 32:40], st[:, 24:32])
                po.wait_ge(qk_ready, 2 * l + 1)
                for dst, lo, hi in ((new_b_k, CKB, CVB), (new_b_v, CVB, CQC), (new_c_k, CKC, CVC), (new_c_v, CVC, 2048)):
                    po.dma_start(dst[0, l].rearrange("t h n -> t (h n)"), PR[:, 0, lo:hi]).then_inc(kv_stored, 16)
                po.wait_ge(kv_stored, 64 * (l + 1))
                po.wait_ge(o_kept, 12 * l + 12)
                for n, w in enumerate((ln1_g, ln1_b)):
                    po.dma_start(LN1[:, n, :], w[l:l + 1, :].broadcast_to([P, D])).then_inc(ln_loaded, 16)
                for s in range(2):
                    rstd(6 * l + 2 + s, st[:, 14:15], st[:, 15:16])
                po.wait_ge(ln_loaded, 32 * (2 * l + 1))
                po.wait_ge(h_ready, 8 * l + 8)
                for n, w in enumerate((ln2_g, ln2_b)):
                    po.dma_start(LN2[:, n, :], w[l:l + 1, :].broadcast_to([P, D])).then_inc(ln_loaded, 16)
                po.wait_ge(tab_ready, l + 1)
                def body(g, start, head, kept=0):
                    if kept:
                        po.wait_ge(sorted_kept, 13 * l + kept)
                    po.wait_ge(gu_done, g + 1)
                    po.tensor_copy(hb[:, :, :], hS[:, :, bass.ds(start, BLK)]).then_inc(hb_ready, 1)

                blocks_of_expert(po, 0, lambda g, start, head: body(g, start, head, 9))
                blocks_of_expert(po, 1, lambda g, start, head: body(g, start, head, 13))
                with po.Fori(2, NE) as e:
                    blocks_of_expert(po, e, body)
                for s in range(2):
                    rstd(6 * l + 4 + s, st[:, 14:15], st[:, 15:16])
            po.wait_ge(kv_stored, 64 * DEPTH)


SMALL = 16 * 25


_INS = ['x_prompt', 'x_sample', 'cache_b_k', 'cache_b_v', 'cache_c_k', 'cache_c_v', 'c', 'c_ctx', 'w_ada', 'b_ada',
        'w_in', 'w_out', 'pool_w', 'pool_scale', 'q_norm', 'k_norm', 'rpb', 'ln1_g', 'ln1_b', 'ln2_g', 'ln2_b',
        'router_g', 'router_g_b', 'router_e', 'router_e_b', 'w_gate', 'w_up', 'w_down']
_OUTS = [(1, 128, 1024), (1, 128, 1024), (1, 2, 128, 2, 64), (1, 2, 128, 2, 64), (1, 2, 128, 6, 64),
         (1, 2, 128, 6, 64)]


def kernel(**inputs):
    import concourse.bacc as _bacc
    from concourse.bass_utils import run_bass_kernel_spmd as _run

    nc = _bacc.Bacc("TRN2", target_bir_lowering=False, num_devices=1)
    arrays, args = {}, []
    for name in _INS:
        a = np.ascontiguousarray(inputs[name])
        arrays[f"in_{name}_dram"] = a
        args.append(nc.dram_tensor(f"in_{name}_dram", a.shape, mybir.dt.from_np(a.dtype), kind="ExternalInput").ap())
    arrays["in_consts_dram"] = shape_constants()
    args.append(nc.dram_tensor("in_consts_dram", (P, CONST_COLS), F32, kind="ExternalInput").ap())
    for i, shape in enumerate(_OUTS):
        args.append(nc.dram_tensor(f"out_{i}_dram", shape, F32, kind="ExternalOutput").ap())
    backbone(nc, *args)
    r = _run(nc, [arrays], core_ids=[0])
    return tuple(r.results[0][f"out_{i}_dram"] for i in range(len(_OUTS)))
```
